# Optimizing a Trainium2 kernel written in Bass

```python
import jax, jax.numpy as jnp
from jax import lax
import numpy as np

D_MODEL = 2048
BATCH = 1
SEQ = 256
DEPTH = 1

Q_BLOCK = 128
HEAD_WIDTH = 128
MLA_HEADS = (D_MODEL // 2) // HEAD_WIDTH
MLA_NOPE_DIM = 128
MLA_ROPE_DIM = 64
MLA_V_DIM = 128
MLA_QK_DIM = MLA_NOPE_DIM + MLA_ROPE_DIM
MLA_Q_RANK = 768
MLA_KV_RANK = 512
MLA_WIDTH = MLA_HEADS * MLA_V_DIM
FOX_HEADS = (D_MODEL // 2) // HEAD_WIDTH
FOX_HEAD_DIM = HEAD_WIDTH
FOX_WIDTH = FOX_HEADS * FOX_HEAD_DIM
D_MIX = MLA_WIDTH + FOX_WIDTH
ROPE_THETA = 10000.0
NORM_EPS = 1e-6
IN_SPLITS = (MLA_Q_RANK, MLA_KV_RANK, MLA_ROPE_DIM, MLA_WIDTH,
             FOX_WIDTH, FOX_WIDTH, FOX_WIDTH, FOX_HEADS, FOX_WIDTH)
D_IN = (MLA_Q_RANK + MLA_KV_RANK + MLA_ROPE_DIM + MLA_WIDTH
        + 4 * FOX_WIDTH + FOX_HEADS)


def _rms_norm(x, g):
    xf = x.astype(jnp.float32)
    y = xf * lax.rsqrt(jnp.mean(xf * xf, axis=-1, keepdims=True) + NORM_EPS)
    return (y * g.astype(jnp.float32)).astype(x.dtype)

def _rope_angles(positions, dim):
    inv_freq = ROPE_THETA ** (-jnp.arange(0, dim, 2, dtype=jnp.float32) / dim)
    ang = positions.astype(jnp.float32)[..., None] * inv_freq
    return jnp.cos(ang), jnp.sin(ang)

def _apply_rope(x, cos, sin):
    xf = x.astype(jnp.float32)
    half = xf.shape[-1] // 2
    x1, x2 = xf[..., :half], xf[..., half:]
    out = jnp.concatenate([x1 * cos - x2 * sin, x2 * cos + x1 * sin], axis=-1)
    return out.astype(x.dtype)

def _causal_block_sweep(score_fn, v):
    b, seq = v.shape[0], v.shape[1]
    n_blocks = seq // Q_BLOCK
    key_pos = jnp.arange(seq)

    def one_block(i):
        start = i * Q_BLOCK
        logits = score_fn(start)
        q_pos = start + jnp.arange(Q_BLOCK)
        logits = jnp.where(key_pos[None, :] <= q_pos[:, None], logits, -jnp.inf)
        p = jax.nn.softmax(logits, axis=-1).astype(v.dtype)
        return jnp.einsum('bhqs,bshd->bqhd', p, v)

    out = lax.map(one_block, jnp.arange(n_blocks))
    return out.transpose(1, 0, 2, 3, 4).reshape(b, seq, -1)

def _mla_branch(q_lat, kv_lat, k_rope_raw, g_q, w_uq, g_kv, w_ukv, cos, sin):
    b, s, _ = q_lat.shape
    q = (_rms_norm(q_lat, g_q) @ w_uq).reshape(b, s, MLA_HEADS, MLA_QK_DIM)
    q_nope = q[..., :MLA_NOPE_DIM]
    q_rope = _apply_rope(q[..., MLA_NOPE_DIM:], cos[:, :, None, :], sin[:, :, None, :])
    kv = (_rms_norm(kv_lat, g_kv) @ w_ukv).reshape(b, s, MLA_HEADS, MLA_NOPE_DIM + MLA_V_DIM)
    k_nope, v = kv[..., :MLA_NOPE_DIM], kv[..., MLA_NOPE_DIM:]
    k_rope = _apply_rope(k_rope_raw, cos, sin)
    scale = MLA_QK_DIM ** -0.5

    def score(start):
        qn = lax.dynamic_slice_in_dim(q_nope, start, Q_BLOCK, axis=1)
        qr = lax.dynamic_slice_in_dim(q_rope, start, Q_BLOCK, axis=1)
        s_nope = jnp.einsum('bqhd,bshd->bhqs', qn, k_nope, preferred_element_type=jnp.float32)
        s_rope = jnp.einsum('bqhr,bsr->bhqs', qr, k_rope, preferred_element_type=jnp.float32)
        return (s_nope + s_rope) * scale

    return _causal_block_sweep(score, v)

def _fox_branch(q, k, v, f_logit, b_forget):
    b, s, _ = q.shape
    q = q.reshape(b, s, FOX_HEADS, FOX_HEAD_DIM)
    k = k.reshape(b, s, FOX_HEADS, FOX_HEAD_DIM)
    v = v.reshape(b, s, FOX_HEADS, FOX_HEAD_DIM)
    log_f = jax.nn.log_sigmoid(f_logit.astype(jnp.float32) + b_forget.astype(jnp.float32))
    c = jnp.cumsum(log_f, axis=1).transpose(0, 2, 1)
    scale = FOX_HEAD_DIM ** -0.5

    def score(start):
        qb = lax.dynamic_slice_in_dim(q, start, Q_BLOCK, axis=1)
        cq = lax.dynamic_slice_in_dim(c, start, Q_BLOCK, axis=2)
        logits = jnp.einsum('bqhd,bshd->bhqs', qb, k, preferred_element_type=jnp.float32) * scale
        return logits + cq[:, :, :, None] - c[:, :, None, :]

    return _causal_block_sweep(score, v)

def _hybrid_layer(x, cos, sin, g_pre, w_in, g_q, w_uq, g_kv, w_ukv, b_forget, w_out, g_post):
    h = _rms_norm(x, g_pre)
    proj = h @ w_in
    split_points = np.cumsum(IN_SPLITS)[:-1].tolist()
    (q_lat, kv_lat, k_rope_raw, gate_mla,
     fq, fk, fv, f_logit, gate_fox) = jnp.split(proj, split_points, axis=-1)
    o_mla = _mla_branch(q_lat, kv_lat, k_rope_raw, g_q, w_uq, g_kv, w_ukv, cos, sin) * jax.nn.silu(gate_mla)
    o_fox = _fox_branch(fq, fk, fv, f_logit, b_forget) * jax.nn.silu(gate_fox)
    o = jnp.concatenate([o_mla, o_fox], axis=-1) @ w_out
    return x + _rms_norm(o, g_post)

def first_inputs(seed: int = 0) -> dict:
    key = jax.random.key(seed)
    ks = jax.random.split(key, 12)
    f32 = jnp.float32
    x = jax.random.normal(ks[0], (BATCH, SEQ, D_MODEL), f32)
    offsets = jax.random.randint(ks[1], (BATCH, 1), 0, 1024, dtype=jnp.int32)
    positions = jnp.arange(SEQ, dtype=jnp.int32)[None, :] + offsets
    g_pre = 1.0 + 0.02 * jax.random.normal(ks[2], (DEPTH, D_MODEL), f32)
    w_in = jax.random.normal(ks[3], (DEPTH, D_MODEL, D_IN), f32) * D_MODEL ** -0.5
    g_q_latent = 1.0 + 0.02 * jax.random.normal(ks[4], (DEPTH, MLA_Q_RANK), f32)
    w_uq = jax.random.normal(ks[5], (DEPTH, MLA_Q_RANK, MLA_HEADS * MLA_QK_DIM), f32) * MLA_Q_RANK ** -0.5
    g_kv_latent = 1.0 + 0.02 * jax.random.normal(ks[6], (DEPTH, MLA_KV_RANK), f32)
    w_ukv = jax.random.normal(ks[7], (DEPTH, MLA_KV_RANK, MLA_HEADS * (MLA_NOPE_DIM + MLA_V_DIM)), f32) * MLA_KV_RANK ** -0.5
    b_forget = 3.0 + 0.1 * jax.random.normal(ks[8], (DEPTH, FOX_HEADS), f32)
    w_out = jax.random.normal(ks[9], (DEPTH, D_MIX, D_MODEL), f32) * D_MIX ** -0.5
    g_post = 1.0 + 0.02 * jax.random.normal(ks[10], (DEPTH, D_MODEL), f32)
    return {"x": x, "positions": positions, "g_pre": g_pre, "w_in": w_in,
            "g_q_latent": g_q_latent, "w_uq": w_uq, "g_kv_latent": g_kv_latent,
            "w_ukv": w_ukv, "b_forget": b_forget, "w_out": w_out, "g_post": g_post}

def first_block(x, positions, g_pre, w_in, g_q_latent, w_uq, g_kv_latent, w_ukv, b_forget, w_out, g_post):
    cos, sin = _rope_angles(positions, MLA_ROPE_DIM)
    for l in range(DEPTH):
        x = _hybrid_layer(x, cos, sin, g_pre[l], w_in[l], g_q_latent[l], w_uq[l],
                          g_kv_latent[l], w_ukv[l], b_forget[l], w_out[l], g_post[l])
    return x


HEAD_DIM = 128
HEADS_PER_GROUP = 4
DILATED_GROUPS = ((128, 1), (512, 4), (2048, 16))
N_ATT_GROUPS = 3
N_ATT_HEADS = N_ATT_GROUPS * HEADS_PER_GROUP
ATT_WIDTH = N_ATT_HEADS * HEAD_DIM
ATT_OUT_WIDTH = HEADS_PER_GROUP * HEAD_DIM
ROPE_DIM = HEAD_DIM // 4
ROPE_THETA_2 = 500000.0
ATT_BLOCK = 128

SG_CHUNK = 128
SG_GROUPS = 12
SG_GROUP_DIM = 128
SG_WIDTH = SG_GROUPS * SG_GROUP_DIM

D_FF = 5632

LN_EPS = 1e-5
IN_WIDTH = 3 * ATT_WIDTH + 2 * SG_WIDTH + 2 * D_MODEL


def rmsnorm(x, g):
    x32 = x.astype(jnp.float32)
    r = x32 * lax.rsqrt(jnp.mean(x32 * x32, axis=-1, keepdims=True) + NORM_EPS)
    return (r * g.astype(jnp.float32)).astype(x.dtype)

def layernorm(x, g, b):
    x32 = x.astype(jnp.float32)
    mu = jnp.mean(x32, axis=-1, keepdims=True)
    var = jnp.mean(jnp.square(x32 - mu), axis=-1, keepdims=True)
    y = (x32 - mu) * lax.rsqrt(var + LN_EPS)
    return (y * g.astype(jnp.float32) + b.astype(jnp.float32)).astype(x.dtype)

def swiglu(x, w_gate, w_up, w_down):
    return (jax.nn.silu(x @ w_gate) * (x @ w_up)) @ w_down

def partial_rope(t, pos):
    half = ROPE_DIM // 2
    inv_freq = ROPE_THETA_2 ** (-jnp.arange(0, ROPE_DIM, 2, dtype=jnp.float32) / ROPE_DIM)
    ang = pos.astype(jnp.float32)[:, None] * inv_freq[None, :]
    ang = ang.reshape((1, t.shape[1]) + (1,) * (t.ndim - 3) + (half,))
    cos = jnp.cos(ang).astype(t.dtype)
    sin = jnp.sin(ang).astype(t.dtype)
    x1 = t[..., :half]
    x2 = t[..., half:ROPE_DIM]
    return jnp.concatenate([x1 * cos - x2 * sin, x2 * cos + x1 * sin, t[..., ROPE_DIM:]], axis=-1)

def dilated_window_attention(q, k, v, window, dilation):
    b, s, h, hd = q.shape
    L = s // dilation
    n_blk = -(-L // ATT_BLOCK)
    Lp = n_blk * ATT_BLOCK
    reach = window // dilation

    def by_residue(t):
        t = t.reshape(b, L, dilation, h, hd).transpose(0, 3, 2, 1, 4)
        t = jnp.pad(t, ((0, 0), (0, 0), (0, 0), (0, Lp - L), (0, 0)))
        return t.reshape(b, h, dilation, n_blk, ATT_BLOCK, hd)

    qb, kb, vb = by_residue(q), by_residue(k), by_residue(v)

    def with_prev(t):
        prev = jnp.pad(t[:, :, :, :-1], ((0, 0), (0, 0), (0, 0), (1, 0), (0, 0), (0, 0)))
        return jnp.concatenate([prev, t], axis=4)

    kw, vw = with_prev(kb), with_prev(vb)
    scores = jnp.einsum('bhrnqd,bhrnkd->bhrnqk', qb, kw).astype(jnp.float32) * (hd ** -0.5)
    qi = jnp.arange(ATT_BLOCK)[None, :, None]
    kj = jnp.arange(2 * ATT_BLOCK)[None, None, :]
    blk = jnp.arange(n_blk)[:, None, None]
    diff = qi + ATT_BLOCK - kj
    key_idx = blk * ATT_BLOCK - ATT_BLOCK + kj
    valid = (diff >= 0) & (diff <= reach) & (key_idx >= 0)
    scores = jnp.where(valid[None, None, None], scores, -jnp.inf)
    m = jnp.max(scores, axis=-1, keepdims=True)
    p = jnp.exp(scores - m)
    l = jnp.sum(p, axis=-1, keepdims=True)
    o = jnp.einsum('bhrnqk,bhrnkd->bhrnqd', p.astype(vw.dtype), vw).astype(jnp.float32) / l

    o = o.reshape(b, h, dilation, Lp, hd)[:, :, :, :L].transpose(0, 3, 2, 1, 4).reshape(b, s, h, hd)

    def stat_back(t):
        t = t.reshape(b, h, dilation, Lp)[:, :, :, :L]
        return t.transpose(0, 3, 2, 1).reshape(b, s, h)

    return o, stat_back(m), stat_back(l)

def hybrid_mixer(h, w_in, sg_ln_g, sg_ln_b, sg_w, sg_b, w_att_out, w_sg_out, w_out):
    b, s, _ = h.shape
    proj = h @ w_in
    splits = np.cumsum([ATT_WIDTH, ATT_WIDTH, ATT_WIDTH, SG_WIDTH, SG_WIDTH, D_MODEL]).tolist()
    q, k, v, u, vs, g_att, g_sg = jnp.split(proj, splits, axis=-1)

    pos = jnp.arange(s)
    q = partial_rope(q.reshape(b, s, N_ATT_GROUPS, HEADS_PER_GROUP, HEAD_DIM), pos)
    k = partial_rope(k.reshape(b, s, N_ATT_GROUPS, HEADS_PER_GROUP, HEAD_DIM), pos)
    v = v.reshape(b, s, N_ATT_GROUPS, HEADS_PER_GROUP, HEAD_DIM)
    outs, maxes, dens = [], [], []
    for gi, (window, dilation) in enumerate(DILATED_GROUPS):
        o_g, m_g, l_g = dilated_window_attention(q[:, :, gi], k[:, :, gi], v[:, :, gi], window, dilation)
        outs.append(o_g)
        maxes.append(m_g)
        dens.append(l_g)
    o_all = jnp.stack(outs)
    m_all = jnp.stack(maxes)
    l_all = jnp.stack(dens)
    w_den = l_all * jnp.exp(m_all - jnp.max(m_all, axis=0, keepdims=True))
    o_att = jnp.sum(w_den[..., None] * o_all, axis=0) / jnp.sum(w_den, axis=0)[..., None]
    y_att = o_att.astype(h.dtype).reshape(b, s, ATT_OUT_WIDTH) @ w_att_out

    u = jax.nn.gelu(u, approximate=False)
    vs = layernorm(jax.nn.gelu(vs, approximate=False), sg_ln_g, sg_ln_b)
    vc = vs.reshape(b, s // SG_CHUNK, SG_CHUNK, SG_GROUPS, SG_GROUP_DIM)
    causal = jnp.tril(jnp.ones((SG_CHUNK, SG_CHUNK), dtype=sg_w.dtype))
    w_sp = sg_w * causal[None]
    spatial = jnp.einsum('gts,bcsgd->bctgd', w_sp, vc) + sg_b.T[None, None, :, :, None]
    y_sg = (u * spatial.reshape(b, s, SG_WIDTH)) @ w_sg_out

    merged = jax.nn.sigmoid(g_att) * y_att + jax.nn.sigmoid(g_sg) * y_sg
    return merged @ w_out

def second_inputs(seed: int = 0) -> dict:
    key = jax.random.key(seed)
    ks = jax.random.split(key, 24)
    f32 = jnp.float32

    def nrm(k, shape, fan_in):
        return jax.random.normal(k, shape, f32) * (fan_in ** -0.5)

    def gain(k, shape):
        return 1.0 + 0.05 * jax.random.normal(k, shape, f32)

    return {
        "x": jax.random.normal(ks[0], (BATCH, SEQ, D_MODEL), f32),
        "ffn1_norm": gain(ks[1], (DEPTH, D_MODEL)),
        "ffn1_w_gate": nrm(ks[2], (DEPTH, D_MODEL, D_FF), D_MODEL),
        "ffn1_w_up": nrm(ks[3], (DEPTH, D_MODEL, D_FF), D_MODEL),
        "ffn1_w_down": nrm(ks[4], (DEPTH, D_FF, D_MODEL), D_FF),
        "mix_norm": gain(ks[5], (DEPTH, D_MODEL)),
        "w_in": nrm(ks[6], (DEPTH, D_MODEL, IN_WIDTH), D_MODEL),
        "sg_ln_g": gain(ks[7], (DEPTH, SG_WIDTH)),
        "sg_ln_b": 0.02 * jax.random.normal(ks[8], (DEPTH, SG_WIDTH), f32),
        "sg_w": nrm(ks[9], (DEPTH, SG_GROUPS, SG_CHUNK, SG_CHUNK), SG_CHUNK),
        "sg_b": gain(ks[10], (DEPTH, SG_GROUPS, SG_CHUNK)),
        "w_att_out": nrm(ks[11], (DEPTH, ATT_OUT_WIDTH, D_MODEL), ATT_OUT_WIDTH),
        "w_sg_out": nrm(ks[12], (DEPTH, SG_WIDTH, D_MODEL), SG_WIDTH),
        "w_out": nrm(ks[13], (DEPTH, D_MODEL, D_MODEL), D_MODEL),
        "ffn2_norm": gain(ks[14], (DEPTH, D_MODEL)),
        "ffn2_w_gate": nrm(ks[15], (DEPTH, D_MODEL, D_FF), D_MODEL),
        "ffn2_w_up": nrm(ks[16], (DEPTH, D_MODEL, D_FF), D_MODEL),
        "ffn2_w_down": nrm(ks[17], (DEPTH, D_FF, D_MODEL), D_FF),
        "final_norm": gain(ks[18], (D_MODEL,)),
    }

def second_block(x, ffn1_norm, ffn1_w_gate, ffn1_w_up, ffn1_w_down, mix_norm, w_in, sg_ln_g, sg_ln_b,
              sg_w, sg_b, w_att_out, w_sg_out, w_out, ffn2_norm, ffn2_w_gate, ffn2_w_up, ffn2_w_down,
              final_norm):
    for i in range(DEPTH):
        x = x + 0.5 * swiglu(rmsnorm(x, ffn1_norm[i]), ffn1_w_gate[i], ffn1_w_up[i], ffn1_w_down[i])
        x = x + hybrid_mixer(rmsnorm(x, mix_norm[i]), w_in[i], sg_ln_g[i], sg_ln_b[i], sg_w[i], sg_b[i],
                             w_att_out[i], w_sg_out[i], w_out[i])
        x = x + 0.5 * swiglu(rmsnorm(x, ffn2_norm[i]), ffn2_w_gate[i], ffn2_w_up[i], ffn2_w_down[i])
    return rmsnorm(x, final_norm)


def setup_inputs(seed=0):
    out = dict(first_inputs(seed))
    for name, value in second_inputs(seed + 1).items():
        if name != "x":
            out[name + "_2"] = value
    return out


def reference(
    x, positions, g_pre, w_in, g_q_latent, w_uq, g_kv_latent, w_ukv, b_forget, w_out, g_post,
    ffn1_norm_2, ffn1_w_gate_2, ffn1_w_up_2, ffn1_w_down_2, mix_norm_2, w_in_2, sg_ln_g_2,
    sg_ln_b_2, sg_w_2, sg_b_2, w_att_out_2, w_sg_out_2, w_out_2, ffn2_norm_2, ffn2_w_gate_2,
    ffn2_w_up_2, ffn2_w_down_2, final_norm_2,
):
    x = first_block(
        x, positions, g_pre, w_in, g_q_latent, w_uq, g_kv_latent, w_ukv, b_forget, w_out,
        g_post,
    )
    return second_block(
        x, ffn1_norm_2, ffn1_w_gate_2, ffn1_w_up_2, ffn1_w_down_2, mix_norm_2, w_in_2,
        sg_ln_g_2, sg_ln_b_2, sg_w_2, sg_b_2, w_att_out_2, w_sg_out_2, w_out_2, ffn2_norm_2,
        ffn2_w_gate_2, ffn2_w_up_2, ffn2_w_down_2, final_norm_2,
    )


_drawn_inputs = setup_inputs


def setup_inputs(seed=0):
    import zlib

    import numpy as np

    out = dict(_drawn_inputs(seed))
    spreads = {}
    factors = {'g_q_latent': 8.0,
     'g_kv_latent': 5.775,
     'g_post': 3.767,
     'ffn1_norm_2': 3.575,
     'mix_norm_2': 2.919,
     'sg_ln_g_2': 6.772,
     'sg_ln_b_2': 30.933,
     'sg_b_2': 4.781,
     'ffn2_norm_2': 4.054,
     'b_forget': 57.032}
    for name, (base, spread) in spreads.items():
        noise = np.random.default_rng([zlib.crc32(name.encode()), seed]).standard_normal(out[name].shape)
        drawn = base * np.exp(spread * noise) if base else spread * noise
        out[name] = __import__('jax').numpy.asarray(drawn.astype(out[name].dtype))
    for name, factor in factors.items():
        out[name] = (out[name] * factor).astype(out[name].dtype)
    return out
```

```python
import math
from contextlib import ExitStack

import concourse.bass as bass
from concourse import mybir

F32 = mybir.dt.float32
F32R = mybir.dt.float32r
I32 = mybir.dt.int32
ACT = mybir.ActivationFunctionType
ALU = mybir.AluOpType
AX = mybir.AxisListType

P = 128
D = 2048
SEQ = 256
HALVES = SEQ // P
W = 512
KD = D // P
CHUNKS = D // W
FF = 5632
KF = FF // P
FF_CHUNKS = FF // W
EPS_RMS = 1e-6
EPS_LN = 1e-5

QR, KVR, ROPE, NOPE = 768, 512, 64, 128
HEADS = 8
QK = NOPE + ROPE
FOX = HEADS * P
C_LAT, C_GM = 0, QR + KVR + ROPE
C_FQ = C_GM + HEADS * P
C_FK, C_FV, C_FL = C_FQ + FOX, C_FQ + 2 * FOX, C_FQ + 3 * FOX
C_GF = C_FL + HEADS
LAT = QR + KVR + ROPE + HEADS
LAT2 = LAT - 2 * W
MLA_SCALE = QK ** -0.5
FOX_SCALE = P ** -0.5
MASKED = -1e30

GROUPS_M = 3
PER_GROUP = 4
ATT_W = GROUPS_M * PER_GROUP * P
SG_GROUPS = 12
SG_W = SG_GROUPS * P
DILATIONS = (1, 4, 16)
MIX_ROPE = P // 4
MIX_SCALE = P ** -0.5
W2_QKV, W2_U, W2_VS, W2_GA, W2_GS = 0, 3 * ATT_W, 3 * ATT_W + SG_W, 3 * ATT_W + 2 * SG_W, 3 * ATT_W + 2 * SG_W + D

TILES = 2
RING = 4
AHEAD = 3
G_D = KD // TILES

GAINS = {"pre": 0, "lat": 16, "ffn1": 26, "mix": 42, "ffn2": 58, "sg_b": 74}
GAIN_ROWS = 86
NORMS = ("pre", "q", "kv", "post", "ffn1", "mix", "ln", "ffn2", "final")

FIRST_UNITS = ([("lat", G_D, W), ("lat", G_D, W), ("lat", G_D, LAT2)]
               + [("uq", QR // P // TILES, W)] * 3 + [("ukv", KVR // P // TILES, W)] * 4
               + [("fox", G_D, W)] * 6 + [("gate", G_D, W)] * 4)
FIRST_GROUPS = sum(g for _, g, _ in FIRST_UNITS)
LAT2_FIRST, LAT2_END = 2 * G_D, 3 * G_D
ALL_GROUPS = (FIRST_GROUPS + CHUNKS * G_D + 2 * (FF_CHUNKS * 2 * G_D + CHUNKS * KF // TILES)
              + 15 * G_D + CHUNKS * (2 * G_D + 2 + 6) + CHUNKS * G_D)

MLA_STEPS = [(5 * h + d, step, h) for h in range(HEADS)
             for d, step in ((0, "heads"), (1, "scores"), (3, "probs"), (4, "values"))]
FOX_STEPS = [(48 + 4 * h + d, step, h) for h in range(HEADS)
             for d, step in ((4, "values"), (0, "heads"), (1, "scores"), (3, "probs"))]
MIX_STEPS = [(8 * h + d, step, h, g) for h in range(PER_GROUP)
             for d, step, g in ((0, "heads", 0), (1, "scores", 0), (1, "heads", 1), (2, "scores", 1),
                                (2, "heads", 2), (3, "scores", 2), (5, "probs", 0), (5, "probs", 1),
                                (6, "probs", 2), (7, "values", 0))]


def two_pi_parts():
    rest, parts = 2 * math.pi, []
    for _ in range(4):
        e = math.floor(math.log2(rest)) - 7
        parts.append(math.floor(rest / 2.0 ** e) * 2.0 ** e)
        rest -= parts[-1]
    return parts + [rest]


def raw_target(group):
    n = 16 * (group // RING + 1)
    if group >= LAT2_FIRST:
        n += 16 * ((min(group, LAT2_END - RING + group % RING) - LAT2_FIRST) // RING + 1)
    return n


class Place:

    def __init__(self):
        self.n = dict(group=0, unit=0, job=0, chunk=0, ready=0, score=0, value=0)
        self.turn, self.adds = None, {}

    def target(self, what, more=0, times=1, ring=1):
        v = times * ((self.n[what] + more) // ring)
        if self.turn is not None and self.adds.get(what):
            v = v + self.turn * (times * self.adds[what] // ring)
        return v

    def loop(self, engine, turns, adds):
        with engine.Fori(0, turns) as i:
            before = dict(self.n)
            self.turn, self.adds = i, adds
            yield i
            for k in self.n:
                assert self.n[k] - before[k] == adds.get(k, 0), k
        for k, v in adds.items():
            self.n[k] += v * (turns - 1)
        self.turn, self.adds = None, {}


def build(nc, x, positions, w_in, w_uq, w_ukv, b_forget, w_out, g_post, ffn1_w_gate_2, ffn1_w_up_2,
          ffn1_w_down_2, w_in_2, sg_ln_g_2, sg_ln_b_2, sg_w_2, w_att_out_2, w_sg_out_2, w_out_2,
          ffn2_w_gate_2, ffn2_w_up_2, ffn2_w_down_2, final_norm_2, gains_by_row, fixed, mix_fixed, out):
    ctx = ExitStack()
    with ctx:
        top = (nc.sbuf_base + 31) // 32 * 32

        def place_at(name, shape, dt, offset):
            size = int(np_prod(shape[1:])) * 4
            assert offset + size <= nc.sbuf_usable_end, (name, offset + size, nc.sbuf_usable_end)
            return nc.alloc_sbuf_tensor_at(name, shape, dt, offset=offset), (offset + size + 31) // 32 * 32

        xres, top = place_at("xres", [P, HALVES, D], F32, top)
        act_hi, top = place_at("act_hi", [P, KD, SEQ], F32R, top)
        act_lo, top = place_at("act_lo", [P, KD, SEQ], F32R, top)
        raw, top = place_at("raw", [P, RING, TILES, W], F32, top)
        whi, top = place_at("whi", [P, RING, TILES, W], F32R, top)
        wlo, top = place_at("wlo", [P, RING, TILES, W], F32R, top)
        fix, top = place_at("fix", [P, 544], F32, top)
        ident, mla_mask, tri, inv_freq = fix[:, 0:128], fix[:, 128:384], fix[:, 384:512], fix[:, 512:544]
        gain_rows, top = place_at("gain_rows", [GAIN_ROWS, P], F32, top)
        gains, top = place_at("gains", [P, GAIN_ROWS], F32, top)
        stats, top = place_at("stats", [P, HALVES, 4, 6], F32, top)
        stats2, top = place_at("stats2", [P, HALVES, 4, 6], F32, top)
        moments, top = place_at("moments", [P, len(NORMS), HALVES, 2], F32, top)
        ms, top = place_at("ms", [P, len(NORMS), HALVES], F32, top)
        root, top = place_at("root", [P, len(NORMS), HALVES], F32, top)
        rs, top = place_at("rs", [P, len(NORMS), HALVES], F32, top)
        soft, top = place_at("soft", [P, 4, HALVES], F32, top)
        spare, top = place_at("spare", [P, HALVES], F32, top)
        region = top

        lat, top = place_at("lat", [P, HALVES, LAT], F32, region)
        kv, top = place_at("kv", [P, HALVES, HEADS * 2 * P], F32, top)
        gpost = kv[:, 0, :]
        gate_tmp = kv[:, 1, 0:HALVES * W].rearrange("p (h n) -> p h n", h=HALVES)
        fox, top = place_at("fox", [P, HALVES, 3 * FOX], F32, top)
        o_sb, top = place_at("o_sb", [P, HALVES, D], F32, top)
        s1, top = place_at("s1", [P, 384], F32, top)
        pt1, top = place_at("pt1", [P, 384], F32, top)
        qkT1, top = place_at("qkT1", [P, 2 * SEQ], F32, top)
        qrT, top = place_at("qrT", [ROPE, SEQ], F32, top)
        pos_i, top = place_at("pos_i", [P, HALVES], I32, top)
        pos_f, top = place_at("pos_f", [P, HALVES], F32, top)
        angle, top = place_at("angle", [P, 4, HALVES, ROPE // 2], F32, top)
        krT = angle[0:ROPE].rearrange("p a h d -> p (a h d)")
        forget, top = place_at("forget", [P, 8, HALVES, HEADS], F32, top)
        ncT, top = place_at("ncT", [HEADS, SEQ], F32, top)
        ones, top = place_at("ones", [P, P], F32, top)
        bfb, top = place_at("bfb", [P, HEADS], F32, top)
        q_at = top
        q, top = place_at("q", [P, HALVES, HEADS * QK], F32, q_at)
        lat_hi, top = place_at("lat_hi", [P, 10, SEQ], F32R, top)
        lat_lo, top = place_at("lat_lo", [P, 10, SEQ], F32R, top)
        o_hi, top = place_at("o_hi", [P, KD, SEQ], F32R, q_at)
        o_lo, top = place_at("o_lo", [P, KD, SEQ], F32R, top)
        rope_tmp = o_sb[:, 0, 0:4 * HEADS * ROPE // 2].rearrange("p (a h d) -> p a h d", a=4, h=HEADS)

        h_hi, top = place_at("h_hi", [P, KF, SEQ], F32R, region)
        h_lo, top = place_at("h_lo", [P, KF, SEQ], F32R, top)
        g_sb, top = place_at("g_sb", [P, HALVES, W], F32, top)
        h_sb, top = place_at("h_sb", [P, HALVES, W], F32, top)
        gfinal, top = place_at("gfinal", [P, D], F32, top)

        sg_hi, top = place_at("sg_hi", [P, SG_GROUPS, SEQ], F32R, region)
        sg_lo, top = place_at("sg_lo", [P, SG_GROUPS, SEQ], F32R, top)
        merged_at = top
        merged_hi, top = place_at("merged_hi", [P, KD, SEQ], F32R, top)
        merged_lo, top = place_at("merged_lo", [P, KD, SEQ], F32R, top)
        qk2, top = place_at("qk2", [P, HALVES, 2 * ATT_W], F32, region)
        assert top == merged_at
        v2, top = place_at("v2", [P, HALVES, ATT_W], F32, top)
        u2, top = place_at("u2", [P, HALVES, SG_W], F32, top)
        vs2, top = place_at("vs2", [P, HALVES, SG_W], F32, top)
        wsp_raw = u2[:, :, :].rearrange("p h n -> p (h n)")[:, 0:SG_W].rearrange("p (g s) -> p g s", g=SG_GROUPS)
        att_hi, top = place_at("att_hi", [P, PER_GROUP, SEQ], F32R, top)
        att_lo, top = place_at("att_lo", [P, PER_GROUP, SEQ], F32R, top)
        att_o, top = place_at("att_o", [P, HALVES, W], F32, top)
        s2, top = place_at("s2", [P, GROUPS_M, 384], F32, top)
        pt2, top = place_at("pt2", [P, GROUPS_M, 384], F32, top)
        qkT2, top = place_at("qkT2", [P, 2 * SEQ], F32, top)
        wspT, top = place_at("wspT", [P, SG_GROUPS, P], F32, top)
        mfix, top = place_at("mfix", [P, 832], F32, top)
        ln_gb, top = place_at("ln_gb", [P, 3 * HALVES * W], F32, top)
        ln_g, ln_b = ln_gb[:, 0:SG_W], ln_gb[:, SG_W:2 * SG_W]
        sig_a, sig_g, mixed = (ln_gb[:, i * HALVES * W:(i + 1) * HALVES * W].rearrange("p (h n) -> p h n", h=HALVES)
                               for i in range(3))
        mix_tmp = s2[:, :, :].rearrange("p g n -> p (g n)")
        mix_tmp2 = pt2[:, :, :].rearrange("p g n -> p (g n)")

        acc = [ctx.enter_context(nc.psum_tensor(f"acc{i}", [P, HALVES, W], F32)) for i in range(2)]
        tr = [ctx.enter_context(nc.psum_tensor(f"tr{i}", [P, W], F32)) for i in range(2)]
        s_ps = ctx.enter_context(nc.psum_tensor("s_ps", [P, W], F32))
        o_ps = ctx.enter_context(nc.psum_tensor("o_ps", [P, W], F32))

        def sem(name):
            return ctx.enter_context(nc.semaphore(name))

        raw_in = [sem(f"raw_in{i}") for i in range(RING)]
        hi_ready = sem("hi_ready")
        lo_ready = sem("lo_ready")
        group_used = sem("group_used")
        acc_free = [sem(f"acc_free{i}") for i in range(2)]
        chunk_ready = sem("chunk_ready")
        chunk_split = sem("chunk_split")
        tr_done = sem("tr_done")
        tr_hi = sem("tr_hi")
        tr_free = [sem(f"tr_free{i}") for i in range(2)]
        x_in = [sem(f"x_in{c}") for c in range(CHUNKS)]
        ident_in, fix_in, rows_in, pos_in = sem("ident_in"), sem("fix_in"), sem("rows_in"), sem("pos_in")
        ones_ready, bias_in = sem("ones_ready"), sem("bias_in")
        ms_ready, root_ready, rs_ready = sem("ms_ready"), sem("root_ready"), sem("rs_ready")
        rope_ready = sem("rope_ready")
        scores_done, scores_used = sem("scores_done"), sem("scores_used")
        max_ready, probs_ready = sem("max_ready"), sem("probs_ready")
        values_done, values_used = sem("values_done"), sem("values_used")
        angle_ready, trig_ready = sem("angle_ready"), sem("trig_ready")
        forget_v, forget_a = sem("forget_v"), sem("forget_a")
        wsp_in, mfix_in, ln_in, gpost_in, gfinal_in = (sem("wsp_in"), sem("mfix_in"), sem("ln_in"),
                                                       sem("gpost_in"), sem("gfinal_in"))
        wsp_ready = sem("wsp_ready")
        final_gained = sem("final_gained")
        ln_centred, ln_done = sem("ln_centred"), sem("ln_done")
        vector_step = sem("vector_step")
        pool_step = sem("pool_step")
        out_ready, out_sent = [sem(f"out_ready{h}") for h in range(HALVES)], sem("out_sent")

        block = ctx.enter_context(nc.Block())

        after_first = FIRST_GROUPS + CHUNKS * G_D
        after_ffn1 = after_first + FF_CHUNKS * 2 * G_D + CHUNKS * KF // TILES
        after_mix_in = after_ffn1 + 15 * G_D
        after_mixer = after_mix_in + CHUNKS * (2 * G_D + 8) + CHUNKS * G_D

        @block.sync
        def _(sp):
            at = Place()

            def load(w, k, col, width=W, extra=None):
                slot = at.n["group"] % RING
                if at.n["group"] >= RING:
                    sp.wait_ge(lo_ready, at.target("group", 1 - RING))
                rows = w[k * TILES * P:(k + 1) * TILES * P, :].rearrange("(t p) n -> p t n", p=P)
                main = width - (HEADS if extra is not None else 0)
                cols = slice(col, col + main) if isinstance(col, int) else bass.ds(col, main)
                sp.dma_start(raw[:, slot, :, 0:main], rows[:, :, cols]).then_inc(raw_in[slot], 16)
                if extra is not None:
                    sp.dma_start(raw[:, slot, :, main:width],
                                 rows[:, :, extra:extra + HEADS]).then_inc(raw_in[slot], 16)
                at.n["group"] += 1

            def unit(w, groups, col, width=W, extra=None):
                for k in range(groups):
                    load(w, k, col, width, extra)
                at.n["unit"] += 1

            def ffn(w_gate, w_up, w_down):
                for i in at.loop(sp, FF_CHUNKS, dict(group=2 * G_D, unit=2)):
                    unit(w_gate, G_D, i * W)
                    unit(w_up, G_D, i * W)
                for c in range(CHUNKS):
                    unit(w_down, KF // TILES, c * W)

            for k in range(G_D):
                if k < CHUNKS:
                    sp.dma_start(xres[:, :, k * W:(k + 1) * W],
                                 x[:, k * W:(k + 1) * W].rearrange("(h p) n -> p h n", p=P)).then_inc(x_in[k], 16)
                load(w_in, k, 0)
            unit(w_in, G_D, W)
            unit(w_in, G_D, 2 * W, LAT2, extra=C_FL)
            for c in range(3):
                unit(w_uq, QR // P // TILES, c * W)
            for c in range(4):
                unit(w_ukv, KVR // P // TILES, c * W)
            for c in range(6):
                unit(w_in, G_D, C_FQ + c * W)
            for c in range(2):
                unit(w_in, G_D, C_GM + c * W)
            for c in range(2):
                unit(w_in, G_D, C_GF + c * W)
            for c in range(CHUNKS):
                unit(w_out, G_D, c * W)
            ffn(ffn1_w_gate_2, ffn1_w_up_2, ffn1_w_down_2)
            unit(w_in_2, G_D, 0)
            for i in at.loop(sp, 4, dict(group=2 * G_D, unit=2)):
                unit(w_in_2, G_D, i * (2 * W) + W)
                unit(w_in_2, G_D, i * (2 * W) + 2 * W)
            for c in range(3):
                unit(w_in_2, G_D, W2_VS + c * W)
            for c in range(3):
                unit(w_in_2, G_D, W2_U + c * W)
            def merge_chunk(col):
                unit(w_in_2, G_D, col + W2_GA)
                unit(w_att_out_2, 2, col)
                unit(w_in_2, G_D, col + W2_GS)
                unit(w_sg_out_2, 6, col)

            merge_chunk(0)
            for i in at.loop(sp, CHUNKS - 1, dict(group=2 * G_D + 8, unit=4)):
                merge_chunk(i * W + W)
            for c in range(CHUNKS):
                unit(w_out_2, G_D, c * W)
            ffn(ffn2_w_gate_2, ffn2_w_up_2, ffn2_w_down_2)
            assert at.n["group"] == ALL_GROUPS
            for c in range(CHUNKS):
                for half in range(HALVES):
                    sp.wait_ge(out_ready[half], c + 1)
                sp.dma_start(out[:, c * W:(c + 1) * W].rearrange("(h p) n -> p h n", p=P),
                             xres[:, :, c * W:(c + 1) * W]).then_inc(out_sent, 16)
            sp.wait_ge(out_sent, 16 * CHUNKS)

        @block.gpsimd
        def _(pool):
            nc.gpsimd.memset(ones[:], 1.0).then_inc(ones_ready, 1)
            pool.dma_start(bfb[:], b_forget[:, :].partition_broadcast(P)).then_inc(bias_in, 16)
            pool.wait_ge(values_done, HEADS)
            pool.dma_start(gpost[:], g_post[:, :].partition_broadcast(P)).then_inc(gpost_in, 16)
            pool.wait_ge(group_used, after_ffn1)
            pool.dma_start(wsp_raw, sg_w_2.rearrange("g t s -> t g s")).then_inc(wsp_in, 16)
            pool.dma_start(mfix[:], mix_fixed).then_inc(mfix_in, 16)
            pool.dma_start(ln_g, sg_ln_g_2[:, :].partition_broadcast(P)).then_inc(ln_in, 16)
            pool.dma_start(ln_b, sg_ln_b_2[:, :].partition_broadcast(P)).then_inc(ln_in, 16)
            pool.wait_ge(ln_in, 32)
            n = 0
            for c in range(SG_W // W):
                cols = slice(c * W, (c + 1) * W)
                pool.wait_ge(ln_centred, c + 1)
                for half in range(HALVES):
                    nc.gpsimd.tensor_tensor(vs2[:, half, cols], vs2[:, half, cols], ln_g[:, cols],
                                            ALU.mult).then_inc(pool_step, 1)
                    n += 1
                    pool.wait_ge(pool_step, n)
                    nc.gpsimd.tensor_tensor(vs2[:, half, cols], vs2[:, half, cols], ln_b[:, cols],
                                            ALU.add).then_inc(ln_done, 1)
            pool.wait_ge(group_used, after_mixer)
            pool.dma_start(gfinal[:], final_norm_2[:, :].partition_broadcast(P)).then_inc(gfinal_in, 16)

        @block.tensor
        def _(pe):
            at = Place()

            def groups(count, hi, lo, width=W, k0=0):
                if at.n["unit"] >= 2:
                    pe.wait_ge(acc_free[at.n["unit"] % 2], at.target("unit", 0, 2, 2))
                if at.n["chunk"]:
                    pe.wait_ge(chunk_split, at.target("chunk"))
                pair = acc[at.n["unit"] % 2]
                for j in range(count):
                    slot = at.n["group"] % RING
                    pe.wait_ge(lo_ready, at.target("group", 1))
                    for t in range(TILES):
                        k = j * TILES + t
                        for half in range(HALVES):
                            tok = slice(half * P, (half + 1) * P)
                            for n, (left, right) in enumerate(((hi, whi), (hi, wlo), (lo, whi))):
                                last = nc.tensor.matmul(
                                    pair[:, half, 0:width], left[:, k, tok], right[:, slot, t, 0:width],
                                    start=(k == 0 and n == 0), stop=(j == count - 1 and t == TILES - 1 and n == 2),
                                    skip_group_check=True)
                    last.then_inc(group_used, 1)
                    at.n["group"] += 1
                    yield j
                at.n["unit"] += 1

            def job(blocks):
                bank = at.n["job"] % 2
                if at.n["job"] >= 2:
                    pe.wait_ge(tr_free[bank], at.target("job", 0, 1, 2))
                for rows, cols, src in blocks:
                    last = nc.tensor.transpose(tr[bank][0:rows, cols], src, ident[0:src.shape[0], 0:src.shape[0]])
                last.then_inc(tr_done, 1)
                at.n["job"] += 1

            def transpose_chunk(src, col=0, tiles=4, from_input=None):
                if from_input is not None:
                    pe.wait_ge(x_in[from_input], 16)
                else:
                    pe.wait_ge(chunk_ready, at.target("ready", 1))
                    at.n["ready"] += 1
                for b in range(tiles // 2):
                    job([(P, slice(t * SEQ + half * P, t * SEQ + half * P + P),
                          src[:, half, col + (2 * b + t) * P:col + (2 * b + t + 1) * P])
                         for t in range(2) for half in range(HALVES)])
                at.n["chunk"] += 1

            def chunk_is_split():
                pe.wait_ge(chunk_split, at.target("chunk"))

            def opening(j, from_input=False):
                if j < CHUNKS:
                    transpose_chunk(xres, j * W, from_input=j if from_input else None)

            def opened(j):
                if j % 2 == 0:
                    later = min(j + 1, CHUNKS) - (j * TILES // 4 + 1)
                    pe.wait_ge(chunk_split, at.n["chunk"] - later)

            def scores(terms_of):
                if at.n["score"]:
                    pe.wait_ge(scores_used, at.n["score"])
                for cols, tok, keys in ((slice(0, 256), slice(P, 2 * P), slice(0, SEQ)),
                                        (slice(256, 384), slice(0, P), slice(0, P))):
                    terms = terms_of(tok, keys)
                    for n, (left, right) in enumerate(terms):
                        last = nc.tensor.matmul(s_ps[:, cols], left, right, start=(n == 0),
                                                stop=(n == len(terms) - 1), skip_group_check=True)
                last.then_inc(scores_done, 1)
                at.n["score"] += 1

            def transposed():
                for back in (1, 2):
                    n = at.n["job"] - back
                    pe.wait_ge(tr_free[n % 2], n // 2 + 1)

            def probs(src):
                job([(P, slice(b * P, (b + 1) * P), src[:, b * P:(b + 1) * P]) for b in range(3)])

            def values(sources):
                transposed()
                if at.n["value"]:
                    pe.wait_ge(values_used, at.n["value"])
                for qb, blocks in ((0, ((2, 0),)), (1, ((0, 0), (1, 1)))):
                    terms = [(pT[:, b * P:(b + 1) * P], v[:, kb, :]) for pT, v in sources for b, kb in blocks]
                    for n, (left, right) in enumerate(terms):
                        last = nc.tensor.matmul(o_ps[:, qb * P:(qb + 1) * P], left, right, start=(n == 0),
                                                stop=(n == len(terms) - 1), skip_group_check=True)
                last.then_inc(values_done, 1)
                at.n["value"] += 1

            def mla_step(step, h):
                if step == "heads":
                    job([(P, slice(half * P, half * P + P), q[:, half, h * QK:h * QK + NOPE]) for half in range(HALVES)]
                        + [(P, slice(SEQ + half * P, SEQ + half * P + P), kv[:, half, h * 2 * P:h * 2 * P + P])
                           for half in range(HALVES)])
                    job([(ROPE, slice(half * P, half * P + P), q[:, half, h * QK + NOPE:(h + 1) * QK])
                         for half in range(HALVES)])
                elif step == "scores":
                    transposed()
                    scores(lambda tok, keys: [(qkT1[:, tok], qkT1[:, SEQ + keys.start:SEQ + keys.stop]),
                                              (qrT[:, tok], krT[:, keys])])
                elif step == "probs":
                    pe.wait_ge(probs_ready, h + 1)
                    probs(s1)
                else:
                    values([(pt1, kv[:, :, h * 2 * P + P:(h + 1) * 2 * P])])

            def fox_step(step, h):
                if step == "heads":
                    job([(P, slice(part * SEQ + half * P, part * SEQ + half * P + P),
                          fox[:, half, part * FOX + h * P:part * FOX + (h + 1) * P])
                         for part in range(2) for half in range(HALVES)])
                elif step == "scores":
                    transposed()
                    scores(lambda tok, keys: [(qkT1[:, tok], qkT1[:, SEQ + keys.start:SEQ + keys.stop]),
                                              (ident[0:HEADS, h:h + 1].to_broadcast([HEADS, P]), ncT[:, keys])])
                elif step == "probs":
                    pe.wait_ge(probs_ready, HEADS + h + 1)
                    probs(s1)
                else:
                    values([(pt1, fox[:, :, 2 * FOX + h * P:2 * FOX + (h + 1) * P])])

            def mix_step(step, h, g):
                c = (g * PER_GROUP + h) * P
                if step == "heads":
                    job([(P, slice(part * SEQ + half * P, part * SEQ + half * P + P),
                          qk2[:, half, part * ATT_W + c:part * ATT_W + c + P])
                         for part in range(2) for half in range(HALVES)])
                elif step == "scores":
                    transposed()
                    scores(lambda tok, keys: [(qkT2[:, tok], qkT2[:, SEQ + keys.start:SEQ + keys.stop])])
                elif step == "probs":
                    if g == 0:
                        pe.wait_ge(probs_ready, 2 * HEADS + h + 1)
                    probs(s2[:, g, :])
                else:
                    values([(pt2[:, i, :], v2[:, :, (i * PER_GROUP + h) * P:(i * PER_GROUP + h + 1) * P])
                            for i in range(GROUPS_M)])

            pe.wait_ge(ident_in, 16)
            pe.wait_ge(rows_in, 16)
            job([(P, slice(0, GAIN_ROWS), gain_rows[:, :])])

            opening(0, from_input=True)
            opened(0)
            for j in groups(G_D, act_hi, act_lo):
                if j + 1 < G_D:
                    opening(j + 1, from_input=True)
                    opened(j + 1)
            for j in groups(G_D, act_hi, act_lo):
                if j == 3:
                    transpose_chunk(lat, 0)
            for j in groups(G_D, act_hi, act_lo, LAT2):
                if j == 3:
                    transpose_chunk(lat, W)
            for c in range(3):
                for j in groups(QR // P // TILES, lat_hi, lat_lo):
                    if (c, j) == (0, 0):
                        transpose_chunk(lat, 2 * W, 2)
            for c in range(4):
                for j in groups(KVR // P // TILES, lat_hi[:, 6:10, :], lat_lo[:, 6:10, :]):
                    if (c, j) == (3, 0):
                        pe.wait_ge(rope_ready, 3)
                        job([(ROPE, slice(half * P, half * P + P), lat[:, half, QR + KVR:QR + KVR + ROPE])
                             for half in range(HALVES)])
            def attention_at(n):
                for where, step, h in MLA_STEPS:
                    if where == n:
                        mla_step(step, h)
                if n == 42:
                    pe.wait_ge(forget_v, 3)
                    pe.wait_ge(fix_in, 16)
                    pe.wait_ge(ones_ready, 1)
                    pe.wait_ge(scores_used, at.n["score"])
                    nc.tensor.matmul(s_ps[:, 0:8], tri, forget[:, 7, 0, :], start=True, stop=True,
                                     skip_group_check=True)
                    nc.tensor.matmul(s_ps[:, 8:16], tri, forget[:, 7, 1, :], start=True, stop=False,
                                     skip_group_check=True)
                    nc.tensor.matmul(s_ps[:, 8:16], ones[:], forget[:, 7, 0, :], start=False, stop=True,
                                     skip_group_check=True).then_inc(scores_done, 1)
                    at.n["score"] += 1
                if n == 44:
                    pe.wait_ge(forget_v, 4)
                    job([(HEADS, slice(half * P, half * P + P), forget[:, 6, half, :]) for half in range(HALVES)])
                for where, step, h in FOX_STEPS:
                    if where == n:
                        fox_step(step, h)

            n = 0
            for c in range(6):
                for j in groups(G_D, act_hi, act_lo):
                    if n == 0:
                        for u in (8, 9):
                            pe.wait_ge(acc_free[u % 2], 2 * (u // 2 + 1))
                    attention_at(n)
                    n += 1
            for c in range(4):
                for j in groups(G_D, act_hi, act_lo):
                    if (c, j) == (0, 0):
                        for u in (14, 15):
                            pe.wait_ge(acc_free[u % 2], 2 * (u // 2 + 1))
                    attention_at(n)
                    n += 1
                    if c and j == 3:
                        transpose_chunk(o_sb, (c - 1) * W)
            for c in range(CHUNKS):
                for j in groups(G_D, o_hi, o_lo):
                    if c == 0 and j == 0:
                        attention_at(n)
                    if c == 0 and j == 3:
                        transpose_chunk(o_sb, 3 * W)
                    if c == 0 and j == 5:
                        chunk_is_split()
            def ffn(first_one):
                if first_one:
                    opening(0)
                    opened(0)
                for j in groups(G_D, act_hi, act_lo):
                    if first_one and j + 1 < G_D:
                        opening(j + 1)
                        opened(j + 1)
                    if not first_one and j == 3:
                        transpose_chunk(xres, 3 * W)
                    if not first_one and j == 5:
                        chunk_is_split()
                for j in groups(G_D, act_hi, act_lo):
                    pass
                for i in at.loop(pe, FF_CHUNKS - 1, dict(group=2 * G_D, unit=2, job=2, chunk=1, ready=1)):
                    for j in groups(G_D, act_hi, act_lo):
                        if j == 3:
                            transpose_chunk(h_sb)
                    for j in groups(G_D, act_hi, act_lo):
                        pass
                for c in range(CHUNKS):
                    for j in groups(KF // TILES, h_hi, h_lo):
                        if j == 3:
                            if c == 0:
                                transpose_chunk(h_sb)
                            elif first_one:
                                transpose_chunk(xres, (c - 1) * W)
                        if c == 0 and j == KF // TILES - 3:
                            chunk_is_split()

            ffn(True)
            for j in groups(G_D, act_hi, act_lo):
                if j == 3:
                    transpose_chunk(xres, 3 * W)
                if j == 5:
                    chunk_is_split()
            for i in at.loop(pe, 4, dict(group=2 * G_D, unit=2)):
                for c in range(2):
                    for j in groups(G_D, act_hi, act_lo):
                        pass
            n = -2 * G_D
            for c in range(6):
                for j in groups(G_D, act_hi, act_lo):
                    if c == 0 and j in (1, 3, 5):
                        g = 4 * (j // 2)
                        pe.wait_ge(wsp_in, 16)
                        job([(P, slice(i * P, (i + 1) * P), wsp_raw[:, g + i, :]) for i in range(4)])
                    if n == 0:
                        pe.wait_ge(rope_ready, 5)
                        for u in (57, 58):
                            pe.wait_ge(acc_free[u % 2], 2 * (u // 2 + 1))
                    for where, step, h, g in MIX_STEPS:
                        if where == n:
                            mix_step(step, h, g)
                    n += 1

            def spatial(b):
                bank = at.n["job"] % 2
                pe.wait_ge(tr_free[bank], at.n["job"] // 2)
                if b == 0:
                    pe.wait_ge(wsp_ready, 3)
                    pe.wait_ge(ln_done, HALVES * SG_W // W)
                for i in range(2):
                    g = 2 * b + i
                    last = nc.tensor.matmul(tr[bank][:, i * SEQ:(i + 1) * SEQ].rearrange("p (c d) -> p c d", c=2),
                                            wspT[:, g, :], vs2[:, :, g * P:(g + 1) * P], start=(i == 0), stop=True,
                                            skip_group_check=True)
                last.then_inc(tr_done, 1)
                at.n["job"] += 1

            def merge_chunk(first_one):
                for j in groups(G_D, act_hi, act_lo):
                    if first_one:
                        if j == 0:
                            transpose_chunk(att_o)
                        if 1 <= j <= 6:
                            spatial(j - 1)
                        if j in (4, 6):
                            transpose_chunk(u2, (j // 2 - 2) * W)
                    elif j == 3:
                        transpose_chunk(mixed)
                for j in groups(2, att_hi, att_lo):
                    if first_one and j == 0:
                        transpose_chunk(u2, 2 * W)
                for j in groups(G_D, act_hi, act_lo):
                    pass
                for j in groups(6, sg_hi, sg_lo):
                    pass

            merge_chunk(True)
            for i in at.loop(pe, CHUNKS - 1, dict(group=2 * G_D + 8, unit=4, job=2, chunk=1, ready=1)):
                merge_chunk(False)
            for c in range(CHUNKS):
                for j in groups(G_D, merged_hi, merged_lo):
                    if j == 3:
                        if c == 0:
                            transpose_chunk(mixed)
                        else:
                            transpose_chunk(xres, (c - 1) * W)
                    if c == 0 and j == 5:
                        chunk_is_split()
            ffn(False)

        @block.scalar
        def _(act):
            at = Place()

            def split_hi(n):
                m = at.n["group"] + n
                if at.turn is None and m >= ALL_GROUPS:
                    return
                width = LAT2 if LAT2_FIRST <= m < LAT2_END else W
                slot = m % RING
                target = raw_target(m)
                if at.turn is not None:
                    target = target + at.turn * (16 * at.adds["group"] // RING)
                act.wait_ge(raw_in[slot], target)
                if m >= RING:
                    act.wait_ge(group_used, at.target("group", n + 1 - RING))
                nc.scalar.activation(whi[:, slot, :, 0:width], raw[:, slot, :, 0:width],
                                     ACT.Copy).then_inc(hi_ready, 1)

            def groups(count):
                for j in range(count):
                    split_hi(AHEAD)
                    at.n["group"] += 1
                    yield j
                at.n["unit"] += 1

            def unit_ready():
                act.wait_ge(group_used, at.target("group"))

            def pair():
                return acc[at.n["unit"] % 2], acc_free[at.n["unit"] % 2]

            def chunk_hi(hi, tile, gain=None, tiles=4):
                for b in range(tiles // 2):
                    bank = at.n["job"] % 2
                    act.wait_ge(tr_done, at.target("job", 1))
                    if gain is None:
                        first = tile + 2 * b
                        cols = slice(first, first + 2) if isinstance(first, int) else bass.ds(first, 2)
                        last = nc.scalar.activation(
                            hi[:, cols, :], tr[bank][:].rearrange("p (t n) -> p t n", t=2), ACT.Copy)
                    else:
                        for t in range(2):
                            k = 2 * b + t
                            last = nc.scalar.activation(hi[:, tile + k, :], tr[bank][:, t * SEQ:(t + 1) * SEQ],
                                                        ACT.Copy, scale=gains[:, gain + k:gain + k + 1])
                    last.then_inc(tr_hi, 1)
                    at.n["job"] += 1
                at.n["chunk"] += 1
                at.n["ready"] = at.n["chunk"] - CHUNKS

            def opening(j, gain):
                if j < CHUNKS:
                    chunk_hi(act_hi, 4 * j, gain + 4 * j)

            def take_root(norm):
                n = NORMS.index(norm)
                act.wait_ge(ms_ready, n + 1)
                nc.scalar.activation(root[:, n, :], ms[:, n, :], ACT.Sqrt).then_inc(root_ready, 1)

            def load_root_table():
                nc.scalar.activation(spare[:], ms[:, 0, :], ACT.Sqrt)

            def scaled(norm, half):
                n = NORMS.index(norm)
                return rs[:, n, half:half + 1]

            def copy_out(dest, cols, norm, width=W):
                unit_ready()
                a, free = pair()
                nc.scalar.activation(dest[:, 0, cols], a[:, 0, 0:width], ACT.Copy,
                                     scale=scaled(norm, 0)).then_inc(free, 1)

            def activate(dest, func, norm):
                unit_ready()
                a, free = pair()
                for half in range(HALVES):
                    last = nc.scalar.activation(dest[:, half, :], a[:, half, :], func, scale=scaled(norm, half))
                    last.then_inc(free, 1)

            def norm_ready(norm):
                act.wait_ge(rs_ready, NORMS.index(norm) + 1)

            def job_out(dest, src_cols, rows=P):
                bank = at.n["job"] % 2
                act.wait_ge(tr_done, at.n["job"] + 1)
                nc.scalar.activation(dest, tr[bank][0:rows, src_cols], ACT.Copy).then_inc(tr_free[bank], 1)
                at.n["job"] += 1

            def softmax(src_of, scale):
                at.n["value"] += 1
                act.wait_ge(max_ready, at.n["value"])
                for qb in range(2):
                    last = nc.scalar.activation(src_of[qb], src_of[qb], ACT.Exp, bias=soft[:, 1, qb:qb + 1],
                                                scale=scale, accum_out=soft[:, 2, qb:qb + 1])
                last.then_inc(probs_ready, 1)

            act.dma_start(gain_rows[:], gains_by_row).then_inc(rows_in, 16)
            act.dma_start(fix[:, 0:P], fixed[:, 0:P]).then_inc(ident_in, 16)
            act.dma_start(fix[:, P:544], fixed[:, P:544]).then_inc(fix_in, 16)
            act.dma_start(pos_i[:], positions.rearrange("a (h p) -> p (a h)", p=P),
                          allow_slow_non_contiguous=True).then_inc(pos_in, 16)
            job_out(gains[:], slice(0, GAIN_ROWS))
            act.wait_ge(tr_free[0], 1)
            opening(0, GAINS["pre"])
            split_hi(0)
            split_hi(1)
            opening(1, GAINS["pre"])
            split_hi(2)
            opening(2, GAINS["pre"])
            for j in groups(G_D):
                if j == 0:
                    opening(3, GAINS["pre"])
                if j == 6:
                    take_root("pre")
            at.n["unit"] -= 1
            norm_ready("pre")
            copy_out(lat, slice(0, W), "pre")
            at.n["unit"] += 1
            for j in groups(G_D):
                if j == 3:
                    chunk_hi(lat_hi, 0, GAINS["lat"])
                if j == 4:
                    act.wait_ge(angle_ready, 1)
                    nc.scalar.activation(angle[:, 2:4], angle[:, 2:4], ACT.Sin).then_inc(trig_ready, 1)
                if j == 7:
                    copy_out(lat, slice(W, 2 * W), "pre")
            for j in groups(G_D):
                if j == 1:
                    take_root("q")
                if j == 3:
                    chunk_hi(lat_hi, 4, GAINS["lat"] + 4)
                if j == 7:
                    copy_out(lat, slice(2 * W, LAT), "pre", LAT2)
            for c in range(3):
                for j in groups(QR // P // TILES):
                    if (c, j) == (0, 0):
                        chunk_hi(lat_hi, 8, GAINS["lat"] + 8, 2)
                    if (c, j) == (0, 1):
                        take_root("kv")
                    if j == QR // P // TILES - 1:
                        norm_ready("q")
                        copy_out(q, slice(c * W, (c + 1) * W), "q")
            for c in range(4):
                for j in groups(KVR // P // TILES):
                    if j == KVR // P // TILES - 1:
                        norm_ready("kv")
                        copy_out(kv, slice(c * W, (c + 1) * W), "kv")
                    if (c, j) == (3, 0):
                        at.n["job"] += 1

            def attention_at(n):
                for steps, is_fox in ((MLA_STEPS, False), (FOX_STEPS, True)):
                    for where, step, h in steps:
                        if where != n:
                            continue
                        if step == "heads":
                            job_out(qkT1[:], slice(0, 2 * SEQ))
                            if not is_fox:
                                at.n["job"] += 1
                        elif step == "scores":
                            softmax((s1[:, 256:384], s1[:, 0:256]), FOX_SCALE if is_fox else MLA_SCALE)
                        elif step == "probs":
                            job_out(pt1[:], slice(0, 384))
                    if not is_fox:
                        if n == 40:
                            act.wait_ge(forget_v, 1)
                            nc.scalar.activation(forget[:, 2], forget[:, 1], ACT.Exp, scale=-1.0).then_inc(forget_a, 1)
                            act.wait_ge(forget_v, 2)
                            nc.scalar.activation(forget[:, 4], forget[:, 3], ACT.Ln).then_inc(forget_a, 1)
                        if n == 44:
                            at.n["job"] += 1

            n = 0
            for c in range(6):
                for j in groups(G_D):
                    attention_at(n)
                    n += 1
                    if j == 7:
                        copy_out(fox, slice(c * W, (c + 1) * W), "pre")
            for c in range(4):
                for j in groups(G_D):
                    attention_at(n)
                    n += 1
                    if c and j == 3:
                        chunk_hi(o_hi, 4 * (c - 1))
                    if j == 7:
                        if c:
                            act.wait_ge(chunk_ready, at.n["ready"])
                        unit_ready()
                        a, free = pair()
                        for half in range(HALVES):
                            nc.scalar.activation(gate_tmp[:, half, :], a[:, half, :], ACT.Silu,
                                                 scale=scaled("pre", half)).then_inc(free, 1)
            for c in range(CHUNKS):
                for j in groups(G_D):
                    if c == 0 and j == 0:
                        attention_at(n)
                    if c == 0 and j == 3:
                        chunk_hi(o_hi, 12)
                    if c == CHUNKS - 1 and j == 5:
                        load_root_table()
            take_root("post")

            def ffn(norm, first_one):
                gain = GAINS[norm]
                if first_one:
                    opening(0, gain)
                for j in groups(G_D):
                    if first_one and j + 1 < G_D:
                        opening(j + 1, gain)
                    if not first_one and j == 3:
                        chunk_hi(act_hi, 12, gain + 12)
                    if j == 6:
                        take_root(norm)
                    if j == 7:
                        norm_ready(norm)
                        activate(g_sb, ACT.Silu, norm)
                for j in groups(G_D):
                    pass
                for i in at.loop(act, FF_CHUNKS - 1, dict(group=2 * G_D, unit=2, job=2, chunk=1, ready=1)):
                    for j in groups(G_D):
                        if j == 3:
                            chunk_hi(h_hi, i * 4)
                        if j == 7:
                            activate(g_sb, ACT.Silu, norm)
                    for j in groups(G_D):
                        pass
                next_gain = GAINS["mix"]
                for c in range(CHUNKS):
                    for j in groups(KF // TILES):
                        if j == 3:
                            if c == 0:
                                chunk_hi(h_hi, KF - 4)
                            elif first_one:
                                chunk_hi(act_hi, 4 * (c - 1), next_gain + 4 * (c - 1))
                        if not first_one and c == CHUNKS - 1 and j == KF // TILES - 3:
                            load_root_table()

            ffn("ffn1", True)
            for j in groups(G_D):
                if j == 3:
                    chunk_hi(act_hi, 12, GAINS["mix"] + 12)
                if j == 6:
                    take_root("mix")
                if j == 7:
                    norm_ready("mix")
                    copy_out(qk2, slice(0, W), "mix")
            for j in groups(G_D):
                if j == 7:
                    copy_out(qk2, slice(W, 2 * W), "mix")
            for i in at.loop(act, 2, dict(group=2 * G_D, unit=2)):
                for c in range(2):
                    for j in groups(G_D):
                        if j == 7:
                            copy_out(qk2, bass.ds(i * (2 * W) + (c + 2) * W, W), "mix")
            for c in range(3):
                for j in groups(G_D):
                    if j == 7:
                        copy_out(v2, slice(c * W, (c + 1) * W), "mix")
            n = -2 * G_D
            for c in range(6):
                for j in groups(G_D):
                    if c == 0 and j in (1, 3, 5):
                        at.n["job"] += 1
                    for where, step, h, g in MIX_STEPS:
                        if where != n:
                            continue
                        if step == "heads":
                            job_out(qkT2[:], slice(0, 2 * SEQ))
                        elif step == "scores" and g == GROUPS_M - 1:
                            softmax((s2[:, :, 256:384], s2[:, :, 0:256]), MIX_SCALE)
                        elif step == "probs":
                            job_out(pt2[:, g, :], slice(0, 384))
                    n += 1
                    if (c, j) == (3, 0):
                        take_root("ln")
                    if j == 7:
                        if c == 3:
                            act.wait_ge(wsp_ready, 3)
                        activate((vs2 if c < 3 else u2)[:, :, c % 3 * W:(c % 3 + 1) * W], ACT.Gelu, "mix")

            def merge_chunk(first_one, i=None):
                for j in groups(G_D):
                    if first_one:
                        if j == 0:
                            chunk_hi(att_hi, 0)
                        if 1 <= j <= 6:
                            at.n["job"] += 1
                        if j in (4, 6):
                            chunk_hi(sg_hi, 4 * (j // 2 - 2))
                    elif j == 3:
                        chunk_hi(merged_hi, i * 4)
                    if j == 7:
                        activate(sig_a, ACT.Sigmoid, "mix")
                for j in groups(2):
                    if first_one and j == 0:
                        chunk_hi(sg_hi, 8)
                for j in groups(G_D):
                    if j == 7:
                        activate(sig_g, ACT.Sigmoid, "mix")
                for j in groups(6):
                    pass

            merge_chunk(True)
            for i in at.loop(act, CHUNKS - 1, dict(group=2 * G_D + 8, unit=4, job=2, chunk=1, ready=1)):
                merge_chunk(False, i)
            for c in range(CHUNKS):
                for j in groups(G_D):
                    if j == 3:
                        if c == 0:
                            chunk_hi(merged_hi, 12)
                        else:
                            chunk_hi(act_hi, 4 * (c - 1), GAINS["ffn2"] + 4 * (c - 1))
            ffn("ffn2", False)
            take_root("final")
            norm_ready("final")
            for c in range(CHUNKS):
                act.wait_ge(final_gained, c + 1)
                cols = slice(c * W, (c + 1) * W)
                nc.scalar.activation(xres[:, 0, cols], xres[:, 0, cols], ACT.Copy,
                                     scale=scaled("final", 0)).then_inc(out_ready[0], 1)

        @block.vector
        def _(dve):
            at = Place()
            steps, rotated = [0], [0]

            def settled(instruction):
                steps[0] += 1
                instruction.then_inc(vector_step, 1)
                dve.wait_ge(vector_step, steps[0])

            def split_lo(n):
                m = at.n["group"] + n
                if at.turn is None and m >= ALL_GROUPS:
                    return
                width = LAT2 if LAT2_FIRST <= m < LAT2_END else W
                slot = m % RING
                dve.wait_ge(hi_ready, at.target("group", n + 1))
                nc.vector.tensor_tensor(wlo[:, slot, :, 0:width], raw[:, slot, :, 0:width],
                                        whi[:, slot, :, 0:width].bitcast(F32), ALU.subtract).then_inc(lo_ready, 1)

            def groups(count):
                for j in range(count):
                    split_lo(AHEAD)
                    at.n["group"] += 1
                    yield j
                at.n["unit"] += 1

            def unit_ready():
                dve.wait_ge(group_used, at.target("group"))

            def pair():
                return acc[at.n["unit"] % 2], acc_free[at.n["unit"] % 2]

            def chunk_lo(hi, lo, tile, gain=None, tiles=4):
                for b in range(tiles // 2):
                    bank = at.n["job"] % 2
                    dve.wait_ge(tr_hi, at.target("chunk_job", 1))
                    if gain is None:
                        first = tile + 2 * b
                        cols = slice(first, first + 2) if isinstance(first, int) else bass.ds(first, 2)
                        last = nc.vector.tensor_tensor(
                            lo[:, cols, :], tr[bank][:].rearrange("p (t n) -> p t n", t=2),
                            hi[:, cols, :].bitcast(F32), ALU.subtract)
                    else:
                        for t in range(2):
                            k = 2 * b + t
                            last = nc.vector.scalar_tensor_tensor(
                                lo[:, tile + k, :], tr[bank][:, t * SEQ:(t + 1) * SEQ], gains[:, gain + k:gain + k + 1],
                                hi[:, tile + k, :].bitcast(F32), ALU.mult, ALU.subtract)
                    last.then_inc(tr_free[bank], 1)
                    at.n["job"] += 1
                    at.n["chunk_job"] += 1
                dve.wait_ge(tr_free[bank], at.target("job", -1, 1, 2) + 1)
                dve.sem_inc(chunk_split, 1)
                at.n["chunk"] += 1
                at.n["ready"] = at.n["chunk"] - CHUNKS

            at.n["chunk_job"] = 0

            def opening(j, gain):
                if j < CHUNKS:
                    chunk_lo(act_hi, act_lo, 4 * j, gain + 4 * j)

            def row_stats(dest, chunk, src, half):
                return nc.vector.bn_stats(dest[:, half, chunk, :], src)

            def mean_square(norm, source, count, eps, centred=False):
                n = NORMS.index(norm)
                for half in range(HALVES):
                    last = nc.vector.bn_aggr(moments[:, n, half, :], source[:, half, 0:count, :])
                settled(last)
                mean, var = moments[:, n, :, 0], moments[:, n, :, 1]
                if centred:
                    nc.vector.tensor_scalar(ms[:, n, :], var, eps, None, ALU.add).then_inc(ms_ready, 1)
                else:
                    settled(nc.vector.tensor_tensor(ms[:, n, :], mean, mean, ALU.mult))
                    nc.vector.scalar_tensor_tensor(ms[:, n, :], ms[:, n, :], eps, var,
                                                   ALU.add, ALU.add).then_inc(ms_ready, 1)

            def row_scale(norm):
                n = NORMS.index(norm)
                dve.wait_ge(root_ready, n + 1)
                nc.vector.reciprocal(rs[:, n, :], root[:, n, :]).then_inc(rs_ready, 1)

            def norm_ready(norm):
                dve.wait_ge(rs_ready, NORMS.index(norm) + 1)

            def scaled(norm, half):
                n = NORMS.index(norm)
                return rs[:, n, half:half + 1]

            def copy_out(dest, cols, norm, width=W):
                unit_ready()
                a, free = pair()
                nc.vector.tensor_scalar(dest[:, 1, cols], a[:, 1, 0:width], scaled(norm, 1), None,
                                        ALU.mult).then_inc(free, 1)

            def unit_out(u):
                dve.wait_ge(acc_free[u % 2], 2 * (u // 2 + 1))

            def job_out(dest, src_cols, rows=P, factor=None):
                bank = at.n["job"] % 2
                dve.wait_ge(tr_done, at.n["job"] + 1)
                if factor is None:
                    last = nc.vector.tensor_copy(dest, tr[bank][0:rows, src_cols])
                else:
                    last = nc.vector.tensor_scalar(dest, tr[bank][0:rows, src_cols], factor, None, ALU.mult)
                last.then_inc(tr_free[bank], 1)
                at.n["job"] += 1

            def rotate(x1, x2, cos, sin, tmp):
                if rotated[0]:
                    dve.wait_ge(rope_ready, rotated[0])
                rotated[0] += 1
                nc.vector.tensor_tensor(tmp[0], x1, cos, ALU.mult)
                nc.vector.tensor_tensor(tmp[1], x2, sin, ALU.mult)
                nc.vector.tensor_tensor(tmp[2], x2, cos, ALU.mult)
                settled(nc.vector.tensor_tensor(tmp[3], x1, sin, ALU.mult))
                nc.vector.tensor_tensor(x1, tmp[0], tmp[1], ALU.subtract)
                nc.vector.tensor_tensor(x2, tmp[2], tmp[3], ALU.add).then_inc(rope_ready, 1)

            def masked_scores(dest, mask, add=None):
                dve.wait_ge(scores_done, at.n["score"] + 1)
                for qb, cols, m in ((1, slice(0, 256), mask), (0, slice(256, 384), mask[:, P:2 * P])):
                    if add is None:
                        last = nc.vector.tensor_tensor(dest[:, cols], s_ps[:, cols], m, ALU.add)
                    else:
                        last = nc.vector.scalar_tensor_tensor(dest[:, cols], s_ps[:, cols], add[qb], m, ALU.add, ALU.add)
                last.then_inc(scores_used, 1)
                at.n["score"] += 1

            def row_max(blocks, axis, scale):
                dve.wait_ge(scores_used, at.n["score"])
                for qb, b in enumerate(blocks):
                    last = nc.vector.tensor_reduce(soft[:, 0, qb:qb + 1], b, axis, ALU.max)
                settled(last)
                nc.vector.tensor_scalar(soft[:, 1, :], soft[:, 0, :], -scale, None, ALU.mult).then_inc(max_ready, 1)

            def values_out(dest, col):
                at.n["value"] += 1
                dve.wait_ge(probs_ready, at.n["value"])
                settled(nc.vector.reciprocal(soft[:, 3, :], soft[:, 2, :]))
                dve.wait_ge(values_done, at.n["value"])
                for qb in range(HALVES):
                    last = nc.vector.tensor_scalar(dest[:, qb, col:col + P], o_ps[:, qb * P:(qb + 1) * P],
                                                   soft[:, 3, qb:qb + 1], None, ALU.mult)
                last.then_inc(values_used, 1)

            def add_residual(c, factor):
                unit_ready()
                a, free = pair()
                cols = slice(c * W, (c + 1) * W)
                nc.vector.scalar_tensor_tensor(xres[:, :, cols], a[:], factor, xres[:, :, cols],
                                               ALU.mult, ALU.add).then_inc(free, 2)
                dve.wait_ge(free, at.target("unit", 0, 2, 2) + 2)
                for half in range(HALVES):
                    last = row_stats(stats, c, xres[:, half, cols], half)
                last.then_inc(chunk_ready, 1)

            at.n["job"] += 1
            dve.wait_ge(tr_free[0], 1)
            opening(0, GAINS["pre"])
            split_lo(0)
            split_lo(1)
            opening(1, GAINS["pre"])
            split_lo(2)
            opening(2, GAINS["pre"])

            def residual_stats(pair_of_chunks):
                for c in (2 * pair_of_chunks, 2 * pair_of_chunks + 1):
                    for half in range(HALVES):
                        last = row_stats(stats, c, xres[:, half, c * W:(c + 1) * W], half)
                settled(last)

            for j in groups(G_D):
                if j == 0:
                    opening(3, GAINS["pre"])
                if j in (4, 5):
                    for c in (2 * j - 8, 2 * j - 7):
                        dve.wait_ge(x_in[c], 16)
                    residual_stats(j - 4)
                if j == 6:
                    mean_square("pre", stats, 4, EPS_RMS)
                    row_scale("pre")
                if j == 7:
                    norm_ready("pre")
                    copy_out(lat, slice(0, W), "pre")
                    dve.wait_ge(acc_free[0], 2)
                    dve.sem_inc(chunk_ready, 1)
            sin, cos = angle[:, 2], angle[:, 3]
            for j in groups(G_D):
                if j == 0:
                    dve.wait_ge(pos_in, 16)
                    dve.wait_ge(fix_in, 16)
                    settled(nc.vector.tensor_copy(pos_f[:], pos_i[:]))
                    for half in range(HALVES):
                        last = nc.vector.tensor_scalar(angle[:, 0, half, :], inv_freq, pos_f[:, half:half + 1], None, ALU.mult)
                    settled(last)
                    magic = 1.5 * 2.0 ** 23
                    settled(nc.vector.tensor_scalar(angle[:, 1], angle[:, 0], 1 / (2 * math.pi), magic, ALU.mult, ALU.add))
                    settled(nc.vector.tensor_scalar(angle[:, 1], angle[:, 1], magic, None, ALU.subtract))
                if j == 1:
                    for part in two_pi_parts():
                        settled(nc.vector.scalar_tensor_tensor(angle[:, 0], angle[:, 1], -part, angle[:, 0],
                                                               ALU.mult, ALU.add))
                if j == 2:
                    limit = 3.1415925
                    nc.vector.tensor_scalar(angle[:, 2], angle[:, 0], limit, -limit, ALU.min, ALU.max)
                    settled(nc.vector.tensor_scalar(angle[:, 3], angle[:, 0], math.pi / 2, None, ALU.add))
                    settled(nc.vector.tensor_scalar(angle[:, 1], angle[:, 3], math.pi, -2 * math.pi, ALU.is_gt, ALU.mult))
                    settled(nc.vector.tensor_tensor(angle[:, 3], angle[:, 3], angle[:, 1], ALU.add))
                    nc.vector.tensor_scalar(angle[:, 3], angle[:, 3], limit, -limit,
                                            ALU.min, ALU.max).then_inc(angle_ready, 1)
                if j == 3:
                    chunk_lo(lat_hi, lat_lo, 0, GAINS["lat"])
                if j == 7:
                    copy_out(lat, slice(W, 2 * W), "pre")
                    dve.wait_ge(acc_free[1], 2)
                    dve.sem_inc(chunk_ready, 1)
            for j in groups(G_D):
                if j == 0:
                    for half in range(HALVES):
                        for i in range(2):
                            last = row_stats(stats2, i, lat[:, half, i * (QR // 2):(i + 1) * (QR // 2)], half)
                    settled(last)
                if j == 1:
                    mean_square("q", stats2, 2, EPS_RMS)
                    row_scale("q")
                if j == 3:
                    chunk_lo(lat_hi, lat_lo, 4, GAINS["lat"] + 4)
                if j == 7:
                    copy_out(lat, slice(2 * W, LAT), "pre", LAT2)
                    dve.wait_ge(acc_free[0], 4)
                    dve.sem_inc(chunk_ready, 1)
            for c in range(3):
                for j in groups(QR // P // TILES):
                    if (c, j) == (0, 0):
                        chunk_lo(lat_hi, lat_lo, 8, GAINS["lat"] + 8, 2)
                    if (c, j) == (0, 1):
                        for half in range(HALVES):
                            last = row_stats(stats2, 0, lat[:, half, QR:QR + KVR], half)
                        settled(last)
                        mean_square("kv", stats2, 1, EPS_RMS)
                        row_scale("kv")
                    if j == QR // P // TILES - 1:
                        copy_out(q, slice(c * W, (c + 1) * W), "q")
            for c in range(4):
                for j in groups(KVR // P // TILES):
                    if j == 0 and c < 2:
                        if c == 0:
                            unit_out(4)
                            unit_out(5)
                            dve.wait_ge(trig_ready, 1)
                        heads = q[:, c, :].rearrange("p (h d) -> p h d", h=HEADS)
                        rotate(heads[:, :, NOPE:NOPE + 32], heads[:, :, NOPE + 32:QK],
                               cos[:, c, :].unsqueeze(1).to_broadcast([P, HEADS, 32]),
                               sin[:, c, :].unsqueeze(1).to_broadcast([P, HEADS, 32]),
                               [rope_tmp[:, i] for i in range(4)])
                    if j == 0 and c == 2:
                        key = lat[:, :, QR + KVR:QR + KVR + ROPE]
                        rotate(key[:, :, 0:32], key[:, :, 32:64], cos, sin,
                               [rope_tmp[:, i, 0:2, :] for i in range(4)])
                    if (c, j) == (3, 0):
                        job_out(krT[:], slice(0, SEQ), ROPE)
                    if j == KVR // P // TILES - 1:
                        copy_out(kv, slice(c * W, (c + 1) * W), "kv")

            def attention_at(n):
                for where, step, h in MLA_STEPS:
                    if where != n:
                        continue
                    if step == "heads":
                        at.n["job"] += 1
                        job_out(qrT[:], slice(0, SEQ), ROPE)
                    elif step == "scores":
                        masked_scores(s1, mla_mask)
                        row_max((s1[:, 256:384], s1[:, 0:256]), AX.X, MLA_SCALE)
                    elif step == "probs":
                        at.n["job"] += 1
                    else:
                        values_out(o_sb, h * P)
                z, az, e, u, l, r, c_s, lf = (forget[:, i] for i in range(8))
                if n == 40:
                    dve.wait_ge(bias_in, 16)
                    for half in range(HALVES):
                        last = nc.vector.tensor_tensor(z[:, half, :], lat[:, half, LAT - HEADS:LAT], bfb[:], ALU.add)
                    settled(last)
                    nc.vector.scalar_tensor_tensor(az, z, -1.0, z, ALU.mult, ALU.max).then_inc(forget_v, 1)
                    dve.wait_ge(forget_a, 1)
                    settled(nc.vector.tensor_scalar(u, e, 1.0, None, ALU.add))
                    dve.sem_inc(forget_v, 1)
                if n == 41:
                    settled(nc.vector.tensor_scalar(r, u, 1.0, None, ALU.subtract))
                    settled(nc.vector.tensor_tensor(r, e, r, ALU.subtract))
                    settled(nc.vector.reciprocal(lf, u))
                    settled(nc.vector.tensor_tensor(r, r, lf, ALU.mult))
                    dve.wait_ge(forget_a, 2)
                    settled(nc.vector.tensor_tensor(r, r, l, ALU.add))
                    nc.vector.scalar_tensor_tensor(lf, z, 0.0, r, ALU.min, ALU.subtract).then_inc(forget_v, 1)
                if n == 42:
                    dve.wait_ge(scores_done, at.n["score"] + 1)
                    nc.vector.tensor_scalar(c_s, s_ps[:, 0:16].rearrange("p (a b) -> p a b", a=2), 1 / FOX_SCALE,
                                            None, ALU.mult).then_inc(scores_used, 1)
                    at.n["score"] += 1
                    dve.wait_ge(scores_used, at.n["score"])
                    dve.sem_inc(forget_v, 1)
                if n == 44:
                    job_out(ncT[:], slice(0, SEQ), HEADS, factor=-1.0)
                for where, step, h in FOX_STEPS:
                    if where != n:
                        continue
                    if step in ("heads", "probs"):
                        at.n["job"] += 1
                    elif step == "scores":
                        masked_scores(s1, mla_mask, [c_s[:, qb, h:h + 1] for qb in range(2)])
                        row_max((s1[:, 256:384], s1[:, 0:256]), AX.X, FOX_SCALE)
                    else:
                        values_out(o_sb, FOX + h * P)

            def gate_chunk(c):
                u = 16 + c
                unit_out(u)
                dve.wait_ge(values_used, at.n["value"])
                cols = slice(c * W, (c + 1) * W)
                nc.vector.tensor_tensor(o_sb[:, :, cols], o_sb[:, :, cols], gate_tmp, ALU.mult).then_inc(chunk_ready, 1)

            n = 0
            for c in range(6):
                for j in groups(G_D):
                    attention_at(n)
                    n += 1
                    if j == 7:
                        copy_out(fox, slice(c * W, (c + 1) * W), "pre")
            for c in range(4):
                for j in groups(G_D):
                    attention_at(n)
                    n += 1
                    if c and j == 3:
                        chunk_lo(o_hi, o_lo, 4 * (c - 1))
                    if j == 7 and c < 3:
                        gate_chunk(c)
            def post_gain(c, a, free):
                cols = slice(c * W, (c + 1) * W)
                for half in range(HALVES):
                    nc.vector.tensor_tensor(o_sb[:, half, cols], a[:, half, :], gpost[:, cols],
                                            ALU.mult).then_inc(free, 1)

            for c in range(CHUNKS):
                for j in groups(G_D):
                    if c == 0 and j == 0:
                        attention_at(n)
                    if c == 0 and j == 1:
                        gate_chunk(3)
                    if c == 0 and j == 3:
                        chunk_lo(o_hi, o_lo, 12)
                    if j == 7:
                        if c == 0:
                            dve.wait_ge(gpost_in, 16)
                        unit_ready()
                        a, free = pair()
                        for half in range(HALVES):
                            last = row_stats(stats2, c, a[:, half, :], half)
                        if c == CHUNKS - 1:
                            settled(last)
                            mean_square("post", stats2, 4, EPS_RMS)
                        else:
                            post_gain(c, a, free)
            row_scale("post")
            unit_out(22)
            norm_ready("post")

            def post_chunk(c):
                cols = slice(c * W, (c + 1) * W)
                for half in range(HALVES):
                    last = nc.vector.scalar_tensor_tensor(xres[:, half, cols], o_sb[:, half, cols], scaled("post", half),
                                                          xres[:, half, cols], ALU.mult, ALU.add)
                last.then_inc(chunk_ready, 1)

            def final_gain(c):
                cols = slice(c * W, (c + 1) * W)
                for half in range(HALVES):
                    last = nc.vector.tensor_tensor(xres[:, half, cols], xres[:, half, cols], gfinal[:, cols], ALU.mult)
                last.then_inc(final_gained, 1)

            def ffn(norm, first_one):
                gain = GAINS[norm]
                if first_one:
                    post_chunk(0)
                    opening(0, gain)
                    post_chunk(1)
                    post_gain(CHUNKS - 1, acc[1], acc_free[1])
                    unit_out(23)
                for j in groups(G_D):
                    if first_one and j + 1 < CHUNKS:
                        opening(j + 1, gain)
                        if j + 2 < CHUNKS:
                            post_chunk(j + 2)
                    if first_one and j in (4, 5):
                        if j == 4:
                            dve.wait_ge(chunk_ready, at.n["ready"])
                        residual_stats(j - 4)
                    if not first_one and j == 3:
                        chunk_lo(act_hi, act_lo, 12, gain + 12)
                    if j == 6:
                        mean_square(norm, stats, 4, EPS_RMS)
                        row_scale(norm)

                def gated():
                    norm_ready(norm)
                    unit_ready()
                    dve.wait_ge(acc_free[(at.n["unit"] - 1) % 2], at.target("unit", -1, 2, 2) + 2)
                    a, free = pair()
                    for half in range(HALVES):
                        last = nc.vector.scalar_tensor_tensor(h_sb[:, half, :], a[:, half, :], scaled(norm, half),
                                                              g_sb[:, half, :], ALU.mult, ALU.mult)
                        last.then_inc(free, 1)
                    dve.wait_ge(free, at.target("unit", 0, 2, 2) + 2)
                    dve.sem_inc(chunk_ready, 1)

                for j in groups(G_D):
                    if j == 7:
                        gated()
                for i in at.loop(dve, FF_CHUNKS - 1, dict(group=2 * G_D, unit=2, job=2, chunk=1, chunk_job=2, ready=1)):
                    for j in groups(G_D):
                        if j == 3:
                            chunk_lo(h_hi, h_lo, i * 4)
                    for j in groups(G_D):
                        if j == 7:
                            gated()
                next_gain = GAINS["mix"]
                for c in range(CHUNKS):
                    for j in groups(KF // TILES):
                        if j == 3:
                            if c == 0:
                                chunk_lo(h_hi, h_lo, KF - 4)
                            elif first_one:
                                chunk_lo(act_hi, act_lo, 4 * (c - 1), next_gain + 4 * (c - 1))
                        if j == KF // TILES - 1:
                            add_residual(c, 0.5)
                            if not first_one:
                                if c == 0:
                                    dve.wait_ge(gfinal_in, 16)
                                dve.wait_ge(chunk_ready, at.n["ready"] + c + 1)
                                if c == CHUNKS - 1:
                                    mean_square("final", stats, 4, EPS_RMS)
                                else:
                                    final_gain(c)

            ffn("ffn1", True)
            for j in groups(G_D):
                if j == 3:
                    chunk_lo(act_hi, act_lo, 12, GAINS["mix"] + 12)
                if j == 6:
                    mean_square("mix", stats, 4, EPS_RMS)
                    row_scale("mix")
                if j == 7:
                    norm_ready("mix")
                    copy_out(qk2, slice(0, W), "mix")
            for j in groups(G_D):
                if j == 7:
                    copy_out(qk2, slice(W, 2 * W), "mix")
            for i in at.loop(dve, 2, dict(group=2 * G_D, unit=2)):
                for c in range(2):
                    for j in groups(G_D):
                        if j == 7:
                            copy_out(qk2, bass.ds(i * (2 * W) + (c + 2) * W, W), "mix")
            for c in range(3):
                for j in groups(G_D):
                    if j == 7:
                        copy_out(v2, slice(c * W, (c + 1) * W), "mix")
            mix_masks = [mfix[:, i * 256:(i + 1) * 256] for i in range(GROUPS_M)]
            mix_cos = mfix[:, 768:800].rearrange("p (h d) -> p h d", h=HALVES)
            mix_sin = mfix[:, 800:832].rearrange("p (h d) -> p h d", h=HALVES)
            n = -2 * G_D
            for c in range(6):
                for j in groups(G_D):
                    if c < 2 and j == 0:
                        if c == 0:
                            unit_out(54)
                            unit_out(55)
                            dve.wait_ge(mfix_in, 16)
                        rows = qk2[:, c, :].rearrange("p (h d) -> p h d", d=P)
                        nh = 2 * GROUPS_M * PER_GROUP
                        tmps = [t.rearrange("p (h d) -> p h d", h=nh)
                                for t in (mix_tmp[:, 0:384], mix_tmp[:, 384:768], mix_tmp[:, 768:1152], mix_tmp2[:, 0:384])]
                        rotate(rows[:, :, 0:16], rows[:, :, 16:32],
                               mix_cos[:, c, :].unsqueeze(1).to_broadcast([P, nh, 16]),
                               mix_sin[:, c, :].unsqueeze(1).to_broadcast([P, nh, 16]), tmps)
                    if c == 0 and j in (1, 3, 5):
                        bank = at.n["job"] % 2
                        g = 4 * (j // 2)
                        dve.wait_ge(tr_done, at.n["job"] + 1)
                        last = nc.vector.tensor_tensor(wspT[:, g:g + 4, :], tr[bank][:].rearrange("p (g t) -> p g t", g=4),
                                                       tri.unsqueeze(1).to_broadcast([P, 4, P]), ALU.mult)
                        last.then_inc(tr_free[bank], 1)
                        dve.wait_ge(tr_free[bank], at.n["job"] // 2 + 1)
                        dve.sem_inc(wsp_ready, 1)
                        at.n["job"] += 1
                    for where, step, h, g in MIX_STEPS:
                        if where != n:
                            continue
                        if step in ("heads", "probs"):
                            at.n["job"] += 1
                        elif step == "scores":
                            masked_scores(s2[:, g, :], mix_masks[g])
                            if g == GROUPS_M - 1:
                                row_max((s2[:, :, 256:384], s2[:, :, 0:256]), AX.XY, MIX_SCALE)
                        else:
                            values_out(att_o, h * P)
                            if h == PER_GROUP - 1:
                                dve.wait_ge(values_used, at.n["value"])
                                dve.sem_inc(chunk_ready, 1)
                    n += 1
                    if c < 3 and j == 7:
                        unit_out(at.n["unit"])
                        for half in range(HALVES):
                            last = row_stats(stats2, c, vs2[:, half, c * W:(c + 1) * W], half)
                        settled(last)
                    if (c, j) == (3, 0):
                        mean_square("ln", stats2, 3, EPS_LN, centred=True)
                        row_scale("ln")
                        norm_ready("ln")
                    if c == 3 and j in (1, 3, 5):
                        cols = slice(j // 2 * W, (j // 2 + 1) * W)
                        i = NORMS.index("ln")
                        for half in range(HALVES):
                            last = nc.vector.tensor_scalar(vs2[:, half, cols], vs2[:, half, cols],
                                                           moments[:, i, half, 0:1], scaled("ln", half),
                                                           ALU.subtract, ALU.mult)
                        last.then_inc(ln_centred, 1)

            def spatial(b):
                bank = at.n["job"] % 2
                dve.wait_ge(tr_done, at.n["job"] + 1)
                if b == 0:
                    unit_out(at.n["unit"] - 1)
                    unit_out(at.n["unit"] - 2)
                for i in range(2):
                    g = 2 * b + i
                    cols = slice(g * P, (g + 1) * P)
                    last = nc.vector.scalar_tensor_tensor(
                        u2[:, :, cols], tr[bank][:, i * SEQ:(i + 1) * SEQ].rearrange("p (c d) -> p c d", c=2),
                        gains[:, GAINS["sg_b"] + g:GAINS["sg_b"] + g + 1], u2[:, :, cols], ALU.add, ALU.mult)
                last.then_inc(tr_free[bank], 1)
                if b % 2:
                    dve.wait_ge(tr_free[bank], at.n["job"] // 2 + 1)
                    dve.sem_inc(chunk_ready, 1)
                at.n["job"] += 1

            def merge_chunk(first_one, i=None):
                for j in groups(G_D):
                    if first_one:
                        if j == 0:
                            chunk_lo(att_hi, att_lo, 0)
                        if 1 <= j <= 6:
                            spatial(j - 1)
                        if j in (4, 6):
                            chunk_lo(sg_hi, sg_lo, 4 * (j // 2 - 2))
                    elif j == 3:
                        chunk_lo(merged_hi, merged_lo, i * 4)
                for j in groups(2):
                    if first_one and j == 0:
                        chunk_lo(sg_hi, sg_lo, 8)
                    if j == 1:
                        unit_ready()
                        dve.wait_ge(acc_free[(at.n["unit"] - 1) % 2], at.target("unit", -1, 2, 2) + 2)
                        a, free = pair()
                        nc.vector.tensor_tensor(mixed[:, :, :], a[:], sig_a, ALU.mult).then_inc(free, 2)
                for j in groups(G_D):
                    pass
                for j in groups(6):
                    if j == 5:
                        unit_ready()
                        dve.wait_ge(acc_free[(at.n["unit"] - 1) % 2], at.target("unit", -1, 2, 2) + 2)
                        dve.wait_ge(acc_free[at.n["unit"] % 2], at.target("unit", -2, 2, 2) + 2)
                        a, free = pair()
                        nc.vector.tensor_tensor(sig_g, a[:], sig_g, ALU.mult).then_inc(free, 2)
                        dve.wait_ge(free, at.target("unit", 0, 2, 2) + 2)
                        nc.vector.tensor_tensor(mixed, mixed, sig_g, ALU.add).then_inc(chunk_ready, 1)

            merge_chunk(True)
            for i in at.loop(dve, CHUNKS - 1, dict(group=2 * G_D + 8, unit=4, job=2, chunk=1, chunk_job=2, ready=1)):
                merge_chunk(False, i)
            for c in range(CHUNKS):
                for j in groups(G_D):
                    if j == 3:
                        if c == 0:
                            chunk_lo(merged_hi, merged_lo, 12)
                        else:
                            chunk_lo(act_hi, act_lo, 4 * (c - 1), GAINS["ffn2"] + 4 * (c - 1))
                    if j == 7:
                        add_residual(c, 1.0)
            ffn("ffn2", False)
            row_scale("final")
            norm_ready("final")
            for c in range(CHUNKS):
                cols = slice(c * W, (c + 1) * W)
                if c == 1:
                    final_gain(CHUNKS - 1)
                dve.wait_ge(final_gained, c + 1)
                nc.vector.tensor_scalar(xres[:, 1, cols], xres[:, 1, cols], scaled("final", 1), None,
                                        ALU.mult).then_inc(out_ready[1], 1)


def np_prod(shape):
    n = 1
    for s in shape:
        n *= s
    return n


_INS = ["x", "positions", "w_in", "w_uq", "w_ukv", "b_forget", "w_out", "g_post", "ffn1_w_gate_2", "ffn1_w_up_2",
        "ffn1_w_down_2", "w_in_2", "sg_ln_g_2", "sg_ln_b_2", "sg_w_2", "w_att_out_2", "w_sg_out_2", "w_out_2",
        "ffn2_w_gate_2", "ffn2_w_up_2", "ffn2_w_down_2", "final_norm_2"]
_DROP = {"x", "w_in", "w_uq", "w_ukv", "w_out", "ffn1_w_gate_2", "ffn1_w_up_2", "ffn1_w_down_2", "w_in_2", "sg_w_2",
         "w_att_out_2", "w_sg_out_2", "w_out_2", "ffn2_w_gate_2", "ffn2_w_up_2", "ffn2_w_down_2"}
_BY_ROW = ["g_pre", "g_q_latent", "g_kv_latent", "ffn1_norm_2", "mix_norm_2", "ffn2_norm_2", "sg_b_2"]


def _constants():
    import numpy as np

    t = np.arange(P)[:, None]
    s = np.arange(P)[None, :]
    f = np.float32
    fixed = np.zeros((P, 544), f)
    fixed[:, 0:128] = np.eye(P)
    fixed[:, 256:384] = np.where(s <= t, 0, MASKED)
    fixed[:, 384:512] = (t <= s)
    fixed[:, 512:544] = f(10000.0) ** (-np.arange(0, ROPE, 2, dtype=f) / f(ROPE))
    mix = np.zeros((P, 832), f)
    for i, d in enumerate(DILATIONS):
        before = (s >= t) if d == 1 else ((t - s) % d == 0)
        mix[:, i * 256:i * 256 + 128] = np.where(before, 0, MASKED)
        mix[:, i * 256 + 128:i * 256 + 256] = np.where((s <= t) & ((t - s) % d == 0), 0, MASKED)
    inv = f(500000.0) ** (-np.arange(0, MIX_ROPE, 2, dtype=f) / f(MIX_ROPE))
    ang = (np.arange(SEQ, dtype=f)[:, None] * inv[None, :]).astype(f).reshape(HALVES, P, MIX_ROPE // 2)
    ang = ang.transpose(1, 0, 2).astype(np.float64)
    mix[:, 768:800] = np.cos(ang).reshape(P, 32)
    mix[:, 800:832] = np.sin(ang).reshape(P, 32)
    return fixed, mix


def kernel(**inputs):
    import numpy as np
    import concourse.bacc as bacc
    from concourse.bass_utils import run_bass_kernel_spmd

    nc = bacc.Bacc("TRN2", target_bir_lowering=False, num_devices=1)
    arrays, args = {}, []
    for name in _INS:
        a = np.ascontiguousarray(inputs[name])
        if name in _DROP:
            a = a.reshape(a.shape[1:])
        if name == "final_norm_2":
            a = a.reshape(1, -1)
        arrays[f"in_{name}"] = a
    arrays["gains_by_row"] = np.concatenate([np.asarray(inputs[name]).reshape(-1, P) for name in _BY_ROW])
    arrays["fixed"], arrays["mix_fixed"] = _constants()
    for name, a in arrays.items():
        args.append(nc.dram_tensor(name, a.shape, mybir.dt.from_np(a.dtype), kind="ExternalInput").ap())
    args.append(nc.dram_tensor("out", (SEQ, D), F32, kind="ExternalOutput").ap())
    build(nc, *args)
    r = run_bass_kernel_spmd(nc, [arrays], core_ids=[0])
    return r.results[0]["out"].reshape(1, SEQ, D)
```
